# Optimizing a Trainium2 kernel written in Bass

```python
import jax, jax.numpy as jnp
from jax import lax
import numpy as np

D_MODEL = 1024
BATCH = 1
SEQ = 512
DEPTH = 1
DEC_BATCH = 1
DEC_SEQ = 1024
PAST_LEN = 128

MIX_WIDTH = D_MODEL
FNET_WIDTH = MIX_WIDTH // 2
FNET_GROUPS = 4
FNET_GROUP_DIM = FNET_WIDTH // FNET_GROUPS
HGRN_WIDTH = MIX_WIDTH - FNET_WIDTH
HGRN_HEADS = 4
HGRN_DK = 128
HGRN_DV = HGRN_WIDTH // HGRN_HEADS
QK_WIDTH = HGRN_HEADS * HGRN_DK
V_WIDTH = HGRN_HEADS * HGRN_DV
IN_WIDTH = FNET_WIDTH + 3 * QK_WIDTH + 2 * V_WIDTH
CHUNK = 64
N_EXPERTS = 16
EC_CAPACITY_FACTOR = 2
D_FF_EXPERT = 2 * D_MODEL
RMS_EPS = 1e-6

kernel_name = "fnet_hgrn2_expert_choice_hybrid_encoder"

def rms_norm(x, w):
    xf = x.astype(jnp.float32)
    y = xf * lax.rsqrt(jnp.mean(xf * xf, axis=-1, keepdims=True) + RMS_EPS)
    return (y * w.astype(jnp.float32)).astype(x.dtype)

def lower_bounds(lb_param):
    p = jax.nn.softmax(lb_param.astype(jnp.float32), axis=0)
    return jnp.maximum(jnp.cumsum(p, axis=0) - p[0:1], 0.0)

def hgrn2_gates(z, lb):
    zf = z.astype(jnp.float32)
    k = (1.0 - lb) * jax.nn.sigmoid(-zf)
    logf = jnp.logaddexp(jnp.log(lb), jnp.log1p(-lb) + jax.nn.log_sigmoid(zf))
    shape = z.shape[:2] + (HGRN_HEADS, HGRN_DK)
    return k.reshape(shape), logf.reshape(shape)

def chunked_gated_recurrence(q, k, v, logf):
    bsz, seq, nh, dk = q.shape
    dv = v.shape[-1]
    n_chunks = seq // CHUNK

    def to_chunks(a):
        return a.reshape(bsz, n_chunks, CHUNK, nh, a.shape[-1]).transpose(1, 0, 3, 2, 4)

    qc, kc, vc, gc = to_chunks(q), to_chunks(k), to_chunks(v), to_chunks(logf)
    causal_in_chunk = jnp.tril(jnp.ones((CHUNK, CHUNK), dtype=bool))[None, None, :, :, None]

    def step(state, inp):
        qb, kb, vb, gb = inp
        b = jnp.cumsum(gb, axis=2)
        diff = b[:, :, :, None, :] - b[:, :, None, :, :]
        decay = jnp.exp(jnp.where(causal_in_chunk, diff, -jnp.inf))
        scores = jnp.einsum("bhtd,bhsd,bhtsd->bhts", qb, kb, decay)
        o = (jnp.einsum("bhts,bhsv->bhtv", scores, vb)
             + jnp.einsum("bhtd,bhdv->bhtv", qb * jnp.exp(b), state))
        b_last = b[:, :, -1]
        state = (jnp.exp(b_last)[..., None] * state
                 + jnp.einsum("bhsd,bhsv->bhdv", kb * jnp.exp(b_last[:, :, None] - b), vb))
        return state, o

    state0 = jnp.zeros((bsz, nh, dk, dv), jnp.float32)
    _, oc = lax.scan(step, state0, (qc, kc, vc, gc))
    return oc.transpose(1, 0, 3, 2, 4).reshape(bsz, seq, nh, dv)

def hybrid_mixer(h, w_in, w_fnet, lb_f, lb_b, out_norm, w_out):
    bsz, seq, _ = h.shape
    proj = h @ w_in
    cuts = np.cumsum([FNET_WIDTH, QK_WIDTH, QK_WIDTH, QK_WIDTH, V_WIDTH]).tolist()
    u, q, zf, zb, iv, g = jnp.split(proj, cuts, axis=-1)

    ug = u.reshape(bsz, seq, FNET_GROUPS, FNET_GROUP_DIM).astype(jnp.float32)
    mixed = jnp.fft.fft2(ug, axes=(1, 3), norm="ortho").real.astype(h.dtype)
    y_fourier = jnp.einsum("blgc,gcd->blgd", mixed, w_fnet).reshape(bsz, seq, FNET_WIDTH)

    qh = jax.nn.silu(q).reshape(bsz, seq, HGRN_HEADS, HGRN_DK)
    vh = iv.reshape(bsz, seq, HGRN_HEADS, HGRN_DV)
    k_f, logf_f = hgrn2_gates(zf, lb_f)
    k_b, logf_b = hgrn2_gates(zb, lb_b)
    o_fwd = chunked_gated_recurrence(qh, k_f, vh, logf_f)
    o_bwd = jnp.flip(chunked_gated_recurrence(jnp.flip(qh, 1), jnp.flip(k_b, 1),
                                              jnp.flip(vh, 1), jnp.flip(logf_b, 1)), 1)
    gate = jax.nn.silu(g.reshape(bsz, seq, HGRN_HEADS, HGRN_DV).astype(jnp.float32))
    y_rec = (rms_norm(o_fwd + o_bwd, out_norm) * gate).astype(h.dtype).reshape(bsz, seq, V_WIDTH)

    return jnp.concatenate([y_fourier, y_rec], axis=-1) @ w_out

def expert_choice_ffn(h, w_router, w_gate, w_up, w_down):
    bsz, seq, d = h.shape
    n_tok = bsz * seq
    cap = EC_CAPACITY_FACTOR * n_tok // N_EXPERTS
    xt = h.reshape(n_tok, d)
    affinity = jax.nn.softmax((xt @ w_router).astype(jnp.float32), axis=-1)
    g, idx = lax.top_k(affinity.T, cap)
    xe = xt[idx]
    he = jax.nn.silu(jnp.einsum("ecd,edf->ecf", xe, w_gate)) * jnp.einsum("ecd,edf->ecf", xe, w_up)
    ye = (jnp.einsum("ecf,efd->ecd", he, w_down) * g[..., None]).astype(xt.dtype)
    out = jnp.zeros_like(xt).at[idx.reshape(-1)].add(ye.reshape(-1, d))
    return out.reshape(bsz, seq, d)

def encoder_trunk(x, lb_f_all, lb_b_all, norm_mix, w_in, w_fnet, hgrn_out_norm, w_out,
                  norm_ffn, w_router, w_gate, w_up, w_down, norm_final):
    for layer in range(DEPTH):
        h = rms_norm(x, norm_mix[layer])
        x = x + hybrid_mixer(h, w_in[layer], w_fnet[layer], lb_f_all[layer], lb_b_all[layer],
                             hgrn_out_norm[layer], w_out[layer])
        h = rms_norm(x, norm_ffn[layer])
        x = x + expert_choice_ffn(h, w_router[layer], w_gate[layer], w_up[layer], w_down[layer])
    return rms_norm(x, norm_final)

def setup_inputs(seed: int = 0) -> dict:
    key = jax.random.key(seed)
    ks = jax.random.split(key, 15)
    f32 = jnp.float32

    def dense(k, shape, fan_in):
        return jax.random.normal(k, shape, f32) * fan_in ** -0.5

    def gain(k, shape):
        return 1.0 + 0.02 * jax.random.normal(k, shape, f32)

    return {
        "x_prompt": jax.random.normal(ks[0], (BATCH, SEQ, D_MODEL), f32),
        "x_sample": jax.random.normal(ks[1], (DEC_BATCH, DEC_SEQ, D_MODEL), f32),
        "norm_mix": gain(ks[2], (DEPTH, D_MODEL)),
        "w_in": dense(ks[3], (DEPTH, D_MODEL, IN_WIDTH), D_MODEL),
        "w_fnet": dense(ks[4], (DEPTH, FNET_GROUPS, FNET_GROUP_DIM, FNET_GROUP_DIM), FNET_GROUP_DIM),
        "lb_fwd": 1.0 + 0.1 * jax.random.normal(ks[5], (DEPTH, QK_WIDTH), f32),
        "lb_bwd": 1.0 + 0.1 * jax.random.normal(ks[6], (DEPTH, QK_WIDTH), f32),
        "hgrn_out_norm": gain(ks[7], (DEPTH, HGRN_DV)),
        "w_out": dense(ks[8], (DEPTH, MIX_WIDTH, D_MODEL), MIX_WIDTH),
        "norm_ffn": gain(ks[9], (DEPTH, D_MODEL)),
        "w_router": dense(ks[10], (DEPTH, D_MODEL, N_EXPERTS), D_MODEL),
        "w_gate": dense(ks[11], (DEPTH, N_EXPERTS, D_MODEL, D_FF_EXPERT), D_MODEL),
        "w_up": dense(ks[12], (DEPTH, N_EXPERTS, D_MODEL, D_FF_EXPERT), D_MODEL),
        "w_down": dense(ks[13], (DEPTH, N_EXPERTS, D_FF_EXPERT, D_MODEL), D_FF_EXPERT),
        "norm_final": gain(ks[14], (D_MODEL,)),
    }

def reference(x_prompt, x_sample, norm_mix, w_in, w_fnet, lb_fwd, lb_bwd, hgrn_out_norm, w_out,
              norm_ffn, w_router, w_gate, w_up, w_down, norm_final):
    lb_f_all = lower_bounds(lb_fwd)
    lb_b_all = lower_bounds(lb_bwd)
    y_prompt = encoder_trunk(x_prompt, lb_f_all, lb_b_all, norm_mix, w_in, w_fnet, hgrn_out_norm, w_out,
                             norm_ffn, w_router, w_gate, w_up, w_down, norm_final)
    y_sample = encoder_trunk(x_sample, lb_f_all, lb_b_all, norm_mix, w_in, w_fnet, hgrn_out_norm, w_out,
                             norm_ffn, w_router, w_gate, w_up, w_down, norm_final)
    return (y_prompt, y_sample)


_drawn_inputs = setup_inputs


def setup_inputs(seed=0):
    import zlib

    import numpy as np

    out = dict(_drawn_inputs(seed))
    spreads = {}
    factors = {'norm_mix': 3.246, 'hgrn_out_norm': 5.335, 'norm_ffn': 3.715, 'norm_final': 2.872}
    for name, (base, spread) in spreads.items():
        noise = np.random.default_rng([zlib.crc32(name.encode()), seed]).standard_normal(out[name].shape)
        drawn = base * np.exp(spread * noise) if base else spread * noise
        out[name] = __import__('jax').numpy.asarray(drawn.astype(out[name].dtype))
    for name, factor in factors.items():
        out[name] = (out[name] * factor).astype(out[name].dtype)
    return out
```

```python
from contextlib import ExitStack

import concourse.bass as bass
from concourse import mybir
import numpy as np

F32 = mybir.dt.float32
F32R = mybir.dt.float32r
U32 = mybir.dt.uint32
U8 = mybir.dt.uint8
ALU = mybir.AluOpType
ACT = mybir.ActivationFunctionType
AX_X = mybir.AxisListType.X

P = 128
D = 1024
KT = D // P
BLK = 512
SEQS = ((0, 512), (512, 1024))
NT = 1536
NB = NT // BLK
TT = NT // P
CH = 4
HEADS = 4
GROUPS = 4
LEVELS = 7
EPS = 1e-6
HEAD_SRC = (4, 5, 1, 2, 3)
NJ = len(HEAD_SRC)
W_HALVES = 2 * (NJ * HEADS + GROUPS)
FIRST_HEAD = 2 * NJ
NE = 16
FF = 2048
CAP_S, CAP_P = 128, 64
CAP = CAP_S + CAP_P
ROWS, PROMPT_ROW = 48, 32
EARLY_ROUNDS = (2, 1, 1, 1, 1, 1, 1, 1, 1)
CHUNKS = 12


def three_products(nc, out, w_hi, w_lo, x_hi, x_lo, start, stop):
    nc.tensor.matmul(out, w_hi, x_hi, start=start, stop=False, skip_group_check=True)
    nc.tensor.matmul(out, w_hi, x_lo, start=False, stop=False, skip_group_check=True)
    return nc.tensor.matmul(out, w_lo, x_hi, start=False, stop=stop, skip_group_check=True)


class HeadWeights:

    def __init__(self, nc, sb, sem, w_heads):
        self.nc, self.w_heads = nc, w_heads
        self.raw = sb("w_raw", [P, 2, KT // 2, P])
        self.hi = sb("w_hi", [P, NJ, KT, P], F32R)
        self.lo = sb("w_lo", [P, NJ, KT, P], F32R)
        self.loaded = [sem(f"w_loaded{i}") for i in range(2)]
        self.hi_done, self.lo_done = sem("w_hi_done"), sem("w_lo_done")

    def half(self, w, m):
        return w[:, m // 2 % NJ, (m % 2) * (KT // 2):(m % 2 + 1) * (KT // 2)]

    def load(self, sp, m):
        if m >= 2:
            sp.wait_ge(self.lo_done, m - 1)
        h, j = m // (2 * NJ), m // 2 % NJ
        src = self.w_heads[h, :, HEAD_SRC[j]] if h < HEADS else self.w_heads[j, :, 0]
        sp.dma_start(self.raw[:, m % 2], src[:, (m % 2) * (KT // 2):(m % 2 + 1) * (KT // 2), :]).then_inc(self.loaded[m % 2], 16)

    def high(self, act, m):
        act.wait_ge(self.loaded[m % 2], 16 * (m // 2 + 1))
        self.nc.scalar.copy(self.half(self.hi, m), self.raw[:, m % 2]).then_inc(self.hi_done, 1)

    def low(self, pool, m):
        pool.wait_ge(self.hi_done, m + 1)
        self.nc.gpsimd.tensor_tensor(self.half(self.lo, m), self.raw[:, m % 2], self.half(self.hi, m).bitcast(F32),
                                     ALU.subtract).then_inc(self.lo_done, 1)


def input_norm_phase(nc, x_dram, norm_mix, identity, weights, hT_hi, hT_lo):
    with ExitStack() as ctx:
        sb = lambda n, s, dt=F32: ctx.enter_context(nc.sbuf_tensor(n, s, dt))
        sem = lambda n: ctx.enter_context(nc.semaphore(n))
        R = 4
        x = sb("x_in", [P, R, D])
        xsq = sb("x_squares", [P, D])
        h = sb("h_rows", [P, 2, D])
        nm = sb("norm_mix_rows", [P, D])
        ident = sb("ident_a", [P, P])
        ss = sb("x_sumsq", [P, TT])
        rms = sb("x_rms", [P, TT])
        rstd = sb("x_rstd", [P, TT])
        eps = sb("eps_a", [P, 1])
        banks = [ctx.enter_context(nc.psum_tensor(f"xT_bank{i}", [P, 4, P], F32)) for i in range(4)]
        x_loaded = [sem(f"x_loaded{i}") for i in range(R)]
        const_loaded, eps_set = sem("const_loaded_a"), sem("eps_set_a")
        squared, rooted, inverted, h_ready = sem("x_squared"), sem("x_rooted"), sem("x_inverted"), sem("h_ready")
        transposed, hi_done, lo_done = sem("h_transposed"), sem("h_hi_done"), sem("h_lo_done")
        with nc.Block() as block:
            @block.sync
            def _(sp):
                sp.dma_start(ident[:], identity).then_inc(const_loaded, 16)
                sp.dma_start(nm[:], norm_mix.partition_broadcast(P)).then_inc(const_loaded, 16)
                for t in range(TT):
                    if t >= R:
                        sp.wait_ge(h_ready, t - R + 1)
                        sp.wait_ge(squared, t - R + 1)
                    sp.dma_start(x[:, t % R], x_dram[t * P:(t + 1) * P]).then_inc(x_loaded[t % R], 16)
                    if t >= 3:
                        weights.load(sp, t - 3)
                for m in range(TT - 3, FIRST_HEAD):
                    weights.load(sp, m)

            @block.gpsimd
            def _(pool):
                for m in range(FIRST_HEAD):
                    weights.low(pool, m)

            @block.scalar
            def _(act):
                act.wait_ge(eps_set, 1)

                def statistics(t):
                    act.wait_ge(x_loaded[t % R], 16 * (t // R + 1))
                    if t >= 1:
                        act.wait_ge(squared, t)
                    nc.scalar.activation(xsq[:], x[:, t % R], ACT.Square, accum_out=ss[:, t:t + 1]).then_inc(squared, 1)
                    act.wait_ge(squared, t + 1)
                    nc.scalar.activation(rms[:, t:t + 1], ss[:, t:t + 1], ACT.Sqrt, scale=1.0 / D,
                                         bias=eps[:]).then_inc(rooted, 1)

                statistics(0)
                for t in range(TT):
                    if t + 1 < TT:
                        statistics(t + 1)
                    if 2 <= t < FIRST_HEAD + 2:
                        weights.high(act, t - 2)
                    for b in range(2):
                        act.wait_ge(transposed, 2 * t + b + 1)
                        nc.scalar.copy(hT_hi[:, 4 * b:4 * b + 4, t * P:(t + 1) * P],
                                       banks[(2 * t + b) % 4][:]).then_inc(hi_done, 1)

            @block.vector
            def _(dve):
                nc.vector.memset(eps[:], EPS).then_inc(eps_set, 1)
                dve.wait_ge(const_loaded, 32)

                def rows(t):
                    dve.wait_ge(rooted, t + 1)
                    nc.vector.reciprocal(rstd[:, t:t + 1], rms[:, t:t + 1]).then_inc(inverted, 1)
                    dve.wait_ge(inverted, t + 1)
                    if t >= 2:
                        dve.wait_ge(transposed, 2 * (t - 1))
                    nc.vector.scalar_tensor_tensor(out=h[:, t % 2], in0=x[:, t % R], scalar=rstd[:, t:t + 1],
                                                   in1=nm[:], op0=ALU.mult, op1=ALU.mult).then_inc(h_ready, 1)

                rows(0)
                for t in range(TT):
                    if t + 1 < TT:
                        rows(t + 1)
                    for b in range(2):
                        dve.wait_ge(hi_done, 2 * t + b + 1)
                        hs = (slice(None), slice(4 * b, 4 * b + 4), slice(t * P, (t + 1) * P))
                        nc.vector.tensor_tensor(hT_lo[hs], banks[(2 * t + b) % 4][:], hT_hi[hs].bitcast(F32),
                                                ALU.subtract).then_inc(lo_done, 1)

            @block.tensor
            def _(pe):
                pe.wait_ge(const_loaded, 32)
                for t in range(TT):
                    pe.wait_ge(h_ready, t + 1)
                    for b in range(2):
                        n = 2 * t + b
                        if n >= 4:
                            pe.wait_ge(lo_done, n - 3)
                        for k in range(4):
                            last = nc.tensor.transpose(banks[n % 4][:, k], h[:, t % 2, (4 * b + k) * P:(4 * b + k + 1) * P],
                                                       ident[:])
                        last.then_inc(transposed, 1)


def heads_phase(nc, weights, lb_params, out_norm, identity, masks, hT_hi, hT_lo, y_dram, u_dram):
    with ExitStack() as ctx:
        sb = lambda n, s, dt=F32: ctx.enter_context(nc.sbuf_tensor(n, s, dt))
        pb = lambda n, s: ctx.enter_context(nc.psum_tensor(n, s, F32))
        sem = lambda n: ctx.enter_context(nc.semaphore(n))
        V, G, Q, ZF, ZB = range(NJ)
        KF, QB, QF, KB = range(4)
        w_hi, w_lo = weights.hi, weights.lo
        kq = [sb(f"kq{b}", [P, 4, BLK]) for b in range(NB)]
        decay = [sb(f"decay{l}", [P, 2, BLK >> l]) for l in range(LEVELS)]
        chunk_decay = sb("chunk_decay", [P, NB, 2, CH])
        q = sb("q", [P, BLK])
        k_sum = sb("k_sum", [P, BLK])
        keys = sb("keys", [P, BLK])
        sig = sb("sig", [P, 2, BLK])
        NG = 4
        gate = sb("gate", [P, NG, BLK])
        v_tok = sb("v_tok", [P, NB, CH, P])
        scores = sb("scores", [P, CH, P])
        state = sb("state", [P, 2, 2, P])
        k_tok = sb("k_tok", [P, 2, CH, P])
        mask = sb("mask", [P, LEVELS, P], U8)
        ident = sb("ident_b", [P, P])
        ones = sb("ones", [P, P])
        onorm = sb("onorm", [P, 1])
        lb = sb("lb", [P, 2, HEADS])
        one_less_lb = sb("one_less_lb", [P, 2, HEADS])
        lbw = sb("lb_work", [P, 4, 2, HEADS])
        rms = sb("o_rms", [P, CH])
        rstd = sb("o_rstd", [P, CH])
        eps = sb("eps_b", [P, 1])
        o_acc = [pb(f"o_acc{b}", [P, CH, P]) for b in range(NB)]
        BANKS = 5
        bank = [pb(f"bank{i}", [P, CH, P]) for i in range(BANKS)]
        PJ, SC, MS = (0, 1), (2, 3), 4

        def proj(n, j):
            return [("begin", n, j), ("proj", n, j)]

        NN = HEADS * NB
        timeline = proj(0, V) + proj(0, G) + [("vt", 0)] + proj(0, Q) + proj(0, ZF) + proj(0, ZB)
        fnet_halves = [e for g in range(GROUPS) for b in range(NB) for e in proj(NN + b, g)]
        FNET_FILL = (2, 1, 1, 2, 1, 1, 1, 1)

        def take_halves(count):
            return [fnet_halves.pop(0) for _ in range(min(count, len(fnet_halves)))]

        for n in range(NN + 1):
            fill = [[] for _ in range(8)]
            if n == NN - 1:
                for s, count in enumerate(FNET_FILL):
                    fill[s] += take_halves(count)
            if n + 1 < NN:
                halves_left = [e for j in (V, G, Q, ZF, ZB) for e in proj(n + 1, j)]
                for s, count in enumerate((1, 1, 1, 1, 1, 2, 2, 1)):
                    fill[s] += halves_left[:count]
                    halves_left = halves_left[count:]
                fill[1] += [("vt", n + 1)]
            if n >= 1 and n % NB != 2:
                h = (n - 1) // NB
                blocks = [0] if n % NB == 1 else [1, 2]
                chunks = [(b, c) for b in blocks for c in range(CH)]
                steps = len(chunks) - 1
                for i in range(steps):
                    for d in range(2):
                        at = chunks if d == 0 else chunks[::-1]
                        fill[i // 2] += [("update", h, d, i, at[i])]
                    for d in range(2):
                        at = chunks if d == 0 else chunks[::-1]
                        fill[i // 2] += [("inter", h, d, i, at[i + 1])]
                    if n == NN:
                        fill[i // 2] += take_halves(1 if i else 2)
                for b in blocks:
                    f = 5 if b == 0 else 4 + (b == 2)
                    last = n == NN
                    fill[f] += [("square", h, b)] + take_halves(2 * last) + [("ss", h, b)]
                    fill[f + 1] += take_halves(1 * last) + [("bc", h, b)]
            for s in range(8):
                if n < NN:
                    timeline.append(("level", n, s))
                timeline += fill[s]
            if n < NN:
                timeline += [("intra", n), ("kt", n, 0), ("kt", n, 1), ("u", n, 0), ("u", n, 1)]
        timeline += fnet_halves

        fill_of, fills, turn = {}, [0] * BANKS, {PJ: 0, SC: 0}
        for ev in timeline:
            if ev[0] == "proj" or ev[0] == "level":
                ring = PJ if ev[0] == "proj" else SC
                i = ring[turn[ring] % 2]
                turn[ring] += 1
            elif ev[0] in ("kt", "u") and ev[2] == 1:
                i = SC[turn[SC] % 2]
                turn[SC] += 1
            elif ev[0] in ("vt", "kt", "u", "ss", "bc"):
                i = MS
            else:
                continue
            fill_of[ev] = (i, fills[i])
            fills[i] += 1
        order = {kind: {ev: i for i, ev in enumerate(e for e in timeline if e[0] == kind)}
                 for kind in ("update", "inter", "square", "ss", "bc")}
        order_of_dir = [{ev: i for i, ev in enumerate(e for e in timeline if e[0] == "update" and e[2] == d)}
                        for d in range(2)]
        inter_of_dir = [{ev: i for i, ev in enumerate(e for e in timeline if e[0] == "inter" and e[2] == d)}
                        for d in range(2)]
        last_inter = {}
        seen = [0, 0]
        for ev in timeline:
            if ev[0] == "inter":
                seen[ev[2]] += 1
                last_inter[(ev[1], 0 if ev[4][0] == 0 else 1)] = tuple(seen)

        const_loaded, const_set = sem("const_loaded_b"), sem("const_set_b")
        mask_loaded = sem("mask_loaded")
        lb_step, lb_exp = sem("lb_step"), sem("lb_exp")
        bank_filled = [sem(f"bank_filled{i}") for i in range(BANKS)]
        bank_read = [sem(f"bank_read{i}") for i in range(BANKS)]
        sig_ready = sem("sig_ready")
        sig_used = [sem(f"sig_used{i}") for i in range(2)]
        dve_step = sem("dve_step")
        q_ready = sem("q_ready")
        kq_made = sem("kq_made")
        kq_up = sem("kq_up")
        keys_ready = sem("keys_ready")
        intra_done = sem("intra_done")
        state_ready = [sem(f"state_ready{d}") for d in range(2)]
        inter_done = [sem(f"inter_done{d}") for d in range(2)]
        squared, weighed = sem("o_squared"), sem("o_weighed")
        diag_ready = sem("diag_ready")
        u_stored = sem("u_stored")
        y_stored = [sem(f"y_stored{i}") for i in range(NG)]

        def filled(eng, ev):
            i, m = fill_of[ev]
            eng.wait_ge(bank_filled[i], m + 1)

        def was_read(eng, ev):
            i, m = fill_of[ev]
            eng.wait_ge(bank_read[i], m + 1)

        def k_tok_unused(eng, ev, d):
            past = timeline[:timeline.index(ev)]
            for kind in ("u", "ss" if d == 0 else "bc"):
                users = [e for e in past if e[0] == kind and (kind != "u" or e[2] == d)]
                if users:
                    filled(eng, users[-1])

        def halves(b, left, right, level, first, count):
            half = 1 << level
            full = kq[b][:].ap[0][0]
            return bass.AP(kq[b][:].tensor, left * BLK + first,
                           [(full, P), (2 * half, count // (2 * half)), ((right - left) * BLK + half, 2), (1, half)])

        with nc.Block() as block:
            @block.sync
            def _(sp):
                sp.dma_start(ident[:], identity).then_inc(const_loaded, 16)
                sp.dma_start(onorm[:], out_norm).then_inc(const_loaded, 16)
                sp.dma_start(lb[:], lb_params).then_inc(const_loaded, 16)
                stores = iter([ev for ev in timeline if ev[0] == "bc"])

                def store(ev):
                    _, h, b = ev
                    was_read(sp, ev)
                    sp.dma_start(y_dram[h, :, b * BLK:(b + 1) * BLK], gate[:, (NB * h + b) % NG])\
                        .then_inc(y_stored[(NB * h + b) % NG], 16)

                for h in range(HEADS):
                    for m in range(max(h * 2 * NJ, FIRST_HEAD), (h + 1) * 2 * NJ):
                        weights.load(sp, m)
                    if h >= 1:
                        for _ in range(NB):
                            store(next(stores))
                for m in range(HEADS * 2 * NJ, W_HALVES):
                    weights.load(sp, m)
                for ev in stores:
                    store(ev)
                for i in range(NG):
                    sp.wait_ge(y_stored[i], 16 * len([n for n in range(NN) if n % NG == i]))

            @block.gpsimd
            def _(pool):
                pool.dma_start(mask[:], masks).then_inc(mask_loaded, 16)
                nc.gpsimd.memset(ones[:], 1.0).then_inc(const_set, 1)
                nc.gpsimd.memset(eps[:], EPS).then_inc(const_set, 1)
                for m in range(FIRST_HEAD, W_HALVES):
                    weights.low(pool, m)
                projections = [ev for ev in timeline if ev[0] == "proj"]
                for i, (_, n, g) in enumerate(projections):
                    if n >= NN:
                        pool.wait_ge(sig_ready, i + 1)
                        pool.dma_start(u_dram[g, :, (n - NN) * BLK:(n - NN + 1) * BLK], sig[:, i % 2]).then_inc(u_stored, 16)
                        pool.wait_ge(u_stored, 16 * (i - NN * NJ + 1))
                        pool.sem_inc(sig_used[i % 2], 1)

            @block.scalar
            def _(act):
                n_sig = 0

                def take_sig():
                    nonlocal n_sig
                    i = n_sig
                    n_sig += 1
                    if i >= 2:
                        act.wait_ge(sig_used[i % 2], i // 2)
                    return sig[:, i % 2]

                def split_weights(h, j):
                    if 2 * (h * NJ + j) < W_HALVES:
                        for f in range(2):
                            weights.high(act, (h * NJ + j) * 2 + f)

                def gather_keys(n, level):
                    if level == 0:
                        act.wait_ge(kq_made, n + 1)
                    else:
                        act.wait_ge(kq_up, n * LEVELS + level)
                        filled(act, ("level", n, level))
                    if level == 0 and n >= 1:
                        filled(act, ("level", n - 1, LEVELS))
                    half = 1 << level
                    nc.scalar.copy(keys[:].rearrange("p (n two h) -> p n two h", two=2, h=half),
                                   halves(n % NB, KF, KB, level, 0, BLK)).then_inc(keys_ready, 1)

                act.wait_ge(lb_step, 1)
                nc.scalar.activation(lbw[:, 1], lbw[:, 0], ACT.Exp).then_inc(lb_exp, 1)
                act.wait_ge(const_set, 2)
                for ev in timeline:
                    kind = ev[0]
                    if kind == "proj":
                        _, n, j = ev
                        i = fill_of[ev][0]
                        x = bank[i][:].rearrange("p c t -> p (c t)")
                        out = take_sig()
                        filled(act, ev)
                        if j == V or n >= NN:
                            nc.scalar.copy(out, x).then_inc(sig_ready, 1)
                            act.wait_ge(sig_ready, n_sig)
                            act.sem_inc(bank_read[i], 1)
                        elif j in (G, Q):
                            nc.scalar.activation(out, x, ACT.Sigmoid).then_inc(sig_ready, 1)
                        else:
                            nc.scalar.activation(out, x, ACT.Sigmoid, scale=-1.0).then_inc(sig_ready, 1)
                            act.wait_ge(sig_ready, n_sig)
                            act.sem_inc(bank_read[i], 1)
                        if n % NB == NB - 1:
                            split_weights(n // NB + 1, j)
                    elif kind == "vt":
                        n = ev[1]
                        filled(act, ev)
                        if n >= NB:
                            filled(act, ("u", n - NB, 0))
                            filled(act, ("u", n - NB, 1))
                            act.wait_ge(intra_done, n - NB + 1)
                        nc.scalar.copy(v_tok[:, n % NB], bank[MS][:]).then_inc(bank_read[MS], 1)
                    elif kind == "level" and ev[2] == 0:
                        n = ev[1]
                        filled(act, ev)
                        act.wait_ge(intra_done, n)
                        i = fill_of[ev][0]
                        nc.scalar.copy(scores[:], bank[i][:]).then_inc(bank_read[i], 1)
                        gather_keys(n, 0)
                    elif kind == "level" and ev[2] < LEVELS:
                        gather_keys(ev[1], ev[2])
                    elif kind == "kt":
                        _, n, d = ev
                        filled(act, ev)
                        k_tok_unused(act, ev, d)
                        i = fill_of[ev][0]
                        nc.scalar.copy(k_tok[:, d], bank[i][:]).then_inc(bank_read[i], 1)
                    elif kind == "u":
                        _, n, d = ev
                        filled(act, ev)
                        i = fill_of[ev][0]
                        nc.scalar.copy(kq[n % NB][:, KF if d == 0 else KB].rearrange("p (c v) -> p c v", c=CH),
                                       bank[i][:]).then_inc(bank_read[i], 1)
                    elif kind == "square":
                        _, h, b = ev
                        for d in range(2):
                            act.wait_ge(inter_done[d], last_inter[(h, min(b, 1))][d])
                        k_tok_unused(act, ev, 0)
                        nc.scalar.activation(k_tok[:, 0], o_acc[b][:], ACT.Square).then_inc(squared, 1)
                    elif kind == "ss":
                        filled(act, ev)
                        i = fill_of[ev][0]
                        nc.scalar.activation(rms[:], bank[i][:, 0, 0:CH], ACT.Sqrt, scale=1.0 / P,
                                             bias=eps[:]).then_inc(bank_read[i], 1)

            @block.vector
            def _(dve):
                own = 0

                def step(ins):
                    nonlocal own
                    own += 1
                    ins.then_inc(dve_step, 1)
                    dve.wait_ge(dve_step, own)

                n_sig = 0

                def sig_in(ev):
                    nonlocal n_sig
                    i = n_sig
                    n_sig += 1
                    dve.wait_ge(sig_ready, i + 1)
                    return sig[:, i % 2], sig_used[i % 2]

                dve.wait_ge(const_loaded, 48)
                dve.wait_ge(mask_loaded, 16)
                nc.vector.tensor_tensor(lbw[:, 0], lb[:], lb[:], ALU.subtract).then_inc(lb_step, 1)
                dve.wait_ge(lb_exp, 1)
                step(nc.vector.reciprocal(lbw[:, 2], lbw[:, 1]))
                step(nc.vector.tensor_tensor(lbw[:, 3], lbw[:, 1], lbw[:, 2], ALU.mult))
                step(nc.vector.tensor_tensor(lbw[:, 0], lbw[:, 3], lbw[:, 3], ALU.subtract))
                step(nc.vector.tensor_scalar(lbw[:, 1], lbw[:, 0], 0.0, None, ALU.max))
                step(nc.vector.tensor_scalar(one_less_lb[:], lbw[:, 1], -1.0, 1.0, ALU.mult, ALU.add))
                for ev in timeline:
                    kind = ev[0]
                    if kind == "proj":
                        _, n, j = ev
                        h, b = n // NB, n % NB
                        i = fill_of[ev][0]
                        x = bank[i][:].rearrange("p c t -> p (c t)")
                        if j == V or n >= NN:
                            n_sig += 1
                        elif j == G:
                            s, used = sig_in(ev)
                            if n >= NG:
                                dve.wait_ge(y_stored[n % NG], 16 * (n // NG))
                            step(nc.vector.tensor_tensor(gate[:, n % NG], s, x, ALU.mult))
                            dve.sem_inc(used, 1)
                            dve.sem_inc(bank_read[i], 1)
                        elif j == Q:
                            s, used = sig_in(ev)
                            if n >= 1:
                                filled(dve, ("level", n - 1, 0))
                            step(nc.vector.tensor_tensor(q[:], s, x, ALU.mult))
                            dve.sem_inc(used, 1)
                            dve.sem_inc(bank_read[i], 1)
                        else:
                            s, used = sig_in(ev)
                            d = 0 if j == ZF else 1
                            if n >= NB and j == ZF:
                                key = (h - 1, min(b, 1))
                                for e in range(2):
                                    dve.wait_ge(inter_done[e], last_inter[key][e])
                            row = kq[b][:, KF if d == 0 else KB]
                            step(nc.vector.tensor_scalar(row, s, one_less_lb[:, d, h:h + 1], None, ALU.mult))
                            dve.sem_inc(used, 1)
                            step(nc.vector.tensor_scalar(decay[0][:, d], row, -1.0, 1.0, ALU.mult, ALU.add))
                            if j == ZB:
                                nc.vector.tensor_tensor(k_sum[:], kq[b][:, KF], kq[b][:, KB], ALU.add).then_inc(q_ready, 1)
                                step(nc.vector.tensor_tensor(kq[b][:, QF], q[:], decay[0][:, 0], ALU.mult))
                                nc.vector.tensor_tensor(kq[b][:, QB], q[:], decay[0][:, 1], ALU.mult).then_inc(kq_made, 1)
                    elif kind == "level" and ev[2] >= 1:
                        _, n, s = ev
                        b, level = n % NB, s - 1
                        half = 1 << level
                        if level == 0:
                            dve.wait_ge(kq_made, n + 1)
                        else:
                            dve.wait_ge(kq_up, n * LEVELS + level)
                        pair = "p r (n two h) -> p r n two h"
                        products = decay[level][:].rearrange("p r (n two) -> p r n two", two=2)
                        shape = [P, 2, BLK // (2 * half), half]
                        right = kq[b][:, QF:KB + 1].rearrange(pair, two=2, h=half)[:, :, :, 1]
                        left = kq[b][:, KF:QB + 1].rearrange(pair, two=2, h=half)[:, :, :, 0]
                        up = decay[level + 1][:] if level + 1 < LEVELS else chunk_decay[:, b]
                        own += 1
                        nc.vector.tensor_tensor(up, products[:, :, :, 0], products[:, :, :, 1], ALU.mult).then_inc(dve_step, 1)
                        filled(dve, ev)
                        own += 1
                        nc.vector.tensor_tensor(right, right, products[:, :, :, 0].unsqueeze(3).to_broadcast(shape), ALU.mult)\
                            .then_inc(dve_step, 1)
                        nc.vector.tensor_tensor(left, left, products[:, :, :, 1].unsqueeze(3).to_broadcast(shape), ALU.mult)\
                            .then_inc(kq_up, 1)
                        if level == 0:
                            was_read(dve, ("level", n, 0))
                        else:
                            was_read(dve, ("level", n, s - 1))
                        i = fill_of[ev][0]
                        nc.vector.copy_predicated(scores[:], mask[:, level].unsqueeze(1).to_broadcast([P, CH, P]),
                                                  bank[i][:]).then_inc(bank_read[i], 1)
                    elif kind == "update":
                        _, h, d, i, (b, c) = ev
                        done = order_of_dir[d][ev]
                        row = kq[b][:, KF if d == 0 else KB, c * P:(c + 1) * P]
                        was_read(dve, ("u", NB * h + b, d))
                        if done >= 2:
                            dve.wait_ge(inter_done[d], done - 1)
                        if i == 0:
                            ins = nc.vector.tensor_copy(state[:, d, done % 2], row)
                        else:
                            dve.wait_ge(state_ready[d], done)
                            ins = nc.vector.scalar_tensor_tensor(
                                out=state[:, d, done % 2], in0=state[:, d, (done - 1) % 2],
                                scalar=chunk_decay[:, b, d, c:c + 1], in1=row, op0=ALU.mult, op1=ALU.add)
                        ins.then_inc(state_ready[d], 1)
                    elif kind == "square":
                        _, h, b = ev
                        m = order["square"][ev]
                        g = gate[:, (NB * h + b) % NG]
                        dve.wait_ge(squared, m + 1)
                        nc.vector.scalar_tensor_tensor(out=g, in0=o_acc[b][:].rearrange("p c t -> p (c t)"),
                                                       scalar=onorm[:], in1=g, op0=ALU.mult, op1=ALU.mult).then_inc(weighed, 1)
                    elif kind == "bc":
                        _, h, b = ev
                        was_read(dve, ("ss", h, b))
                        k_tok_unused(dve, ev, 1)
                        step(nc.vector.reciprocal(rstd[:], rms[:]))
                        for c in range(CH):
                            last = nc.vector.tensor_scalar(k_tok[:, 1, c], ident[:], rstd[:, c:c + 1], None, ALU.mult)
                        last.then_inc(diag_ready, 1)
                        i = fill_of[ev][0]
                        g = gate[:, (NB * h + b) % NG]
                        dve.wait_ge(weighed, order["bc"][ev] + 1)
                        filled(dve, ev)
                        nc.vector.tensor_tensor(g, g, bank[i][:].rearrange("p c t -> p (c t)"), ALU.mult)\
                            .then_inc(bank_read[i], 1)

            @block.tensor
            def _(pe):
                n_sig = 0
                pe.wait_ge(const_loaded, 48)
                pe.wait_ge(const_set, 2)
                v_sig = {}
                for ev in timeline:
                    kind = ev[0]
                    if kind == "begin":
                        i, m = fill_of[("proj",) + ev[1:]]
                    elif ev in fill_of:
                        i, m = fill_of[ev]
                    if kind == "begin" or kind in ("level", "vt", "kt", "u", "ss", "bc"):
                        if m:
                            pe.wait_ge(bank_read[i], m)
                    if kind in ("begin", "proj"):
                        _, n, j = ev
                        h, b = n // NB, n % NB
                        if kind == "begin":
                            if j == V:
                                v_sig[n] = n_sig
                            n_sig += 1
                        if b == 0:
                            pe.wait_ge(weights.lo_done, 2 * (h * NJ + j) + 2)
                        cols = slice(b * BLK, (b + 1) * BLK)
                        out = bank[i][:].rearrange("p c t -> p (c t)")
                        for k in range(KT // 2) if kind == "begin" else range(KT // 2, KT):
                            last = three_products(nc, out, w_hi[:, j, k], w_lo[:, j, k], hT_hi[:, k, cols],
                                                  hT_lo[:, k, cols], k == 0, k == KT - 1)
                        if kind == "proj":
                            last.then_inc(bank_filled[i], 1)
                    elif kind == "vt":
                        n = ev[1]
                        s = v_sig[n]
                        pe.wait_ge(sig_ready, s + 1)
                        for c in range(CH):
                            last = nc.tensor.transpose(bank[i][:, c], sig[:, s % 2, c * P:(c + 1) * P], ident[:])
                        last.then_inc(bank_filled[i], 1)
                        pe.wait_ge(bank_filled[i], m + 1)
                        pe.sem_inc(sig_used[s % 2], 1)
                    elif kind == "level":
                        _, n, s = ev
                        b = n % NB
                        if s == 0:
                            pe.wait_ge(q_ready, n + 1)
                        else:
                            pe.wait_ge(keys_ready, n * LEVELS + s)
                        for c in range(CH):
                            if s == 0:
                                k, qs = k_sum[:, c * P:(c + 1) * P], q[:, c * P:(c + 1) * P]
                            else:
                                k, qs = keys[:, c * P:(c + 1) * P], halves(b, QB, QF, s - 1, c * P, P)
                            last = nc.tensor.matmul(bank[i][:, c], k, qs, start=(c == 0), stop=(c == CH - 1),
                                                    skip_group_check=True)
                        last.then_inc(bank_filled[i], 1)
                    elif kind == "intra":
                        n = ev[1]
                        b = n % NB
                        was_read(pe, ("level", n, LEVELS))
                        was_read(pe, ("vt", n))
                        squares = [e for e in order["square"] if e[2] == b and NB * e[1] + b < n]
                        if squares:
                            pe.wait_ge(weighed, order["square"][squares[-1]] + 1)
                        for c in range(CH):
                            last = nc.tensor.matmul(o_acc[b][:, c], v_tok[:, b, c], scores[:, c], start=(c == 0), stop=False,
                                                    skip_group_check=True)
                        last.then_inc(intra_done, 1)
                    elif kind == "kt":
                        _, n, d = ev
                        b = n % NB
                        pe.wait_ge(kq_up, (n + 1) * LEVELS)
                        for c in range(CH):
                            last = nc.tensor.transpose(bank[i][:, c], kq[b][:, KF if d == 0 else KB, c * P:(c + 1) * P], ident[:])
                        last.then_inc(bank_filled[i], 1)
                    elif kind == "u":
                        _, n, d = ev
                        b = n % NB
                        was_read(pe, ("kt", n, d))
                        for c in range(CH):
                            last = nc.tensor.matmul(bank[i][:, c], k_tok[:, d, c], v_tok[:, b, c], start=(c == 0),
                                                    stop=(c == CH - 1), skip_group_check=True)
                        last.then_inc(bank_filled[i], 1)
                    elif kind == "inter":
                        _, h, d, _, (b, c) = ev
                        done = inter_of_dir[d][ev]
                        pe.wait_ge(state_ready[d], done + 1)
                        nc.tensor.matmul(o_acc[b][:, c], state[:, d, done % 2],
                                         kq[b][:, QF if d == 0 else QB, c * P:(c + 1) * P],
                                         start=False, stop=True, skip_group_check=True).then_inc(inter_done[d], 1)
                    elif kind == "ss":
                        pe.wait_ge(squared, order["ss"][ev] + 1)
                        for c in range(CH):
                            last = nc.tensor.matmul(bank[i][:, 0, c:c + 1], k_tok[:, 0, c], ones[:, 0:1], start=(c == 0),
                                                    stop=(c == CH - 1), skip_group_check=True)
                        last.then_inc(bank_filled[i], 1)
                    elif kind == "bc":
                        pe.wait_ge(diag_ready, order["bc"][ev] + 1)
                        for c in range(CH):
                            last = nc.tensor.matmul(bank[i][:, c], ones[:], k_tok[:, 1, c], start=(c == 0),
                                                    stop=(c == CH - 1), skip_group_check=True)
                        last.then_inc(bank_filled[i], 1)


def fourier_phase(nc, u_dram, w_fnet, channel_dft, tables, w_out, hT_hi, hT_lo, u_space, wo_hi, wo_lo,
                  y_dram):
    NTAB = sum((n // BLK) * (n // 2 // P) * 2 for _, n in SEQS)
    HALF_TILES = TT // 2
    with ExitStack() as ctx:
        sb = lambda n, s, dt=F32: ctx.enter_context(nc.sbuf_tensor(n, s, dt))
        sem = lambda n: ctx.enter_context(nc.semaphore(n))
        wo_raw = sb("wo_raw", [P, 2, D])
        uT = u_space[:, 0:6].rearrange("p a d -> p (a d)").rearrange("p (g t) -> p g t", t=NT)
        even = u_space[:, KT:KT + 3].rearrange("p a d -> p (a d)").rearrange("p (g t) -> p g t", t=NT // 2)
        wf = sb("wf", [P, GROUPS, P])
        dft = sb("dft", [P, 2, P])
        m = sb("m", [P, GROUPS, 2, P])
        RT = 4
        tab = sb("tab", [P, RT, 2, BLK], F32R)
        out = sb("f_out", [P, 4, BLK])
        banks = [ctx.enter_context(nc.psum_tensor(f"f_bank{i}", [P, BLK], F32)) for i in range(8)]
        p_hi = hT_hi[:].rearrange("p k (a n) -> p (k a) n", n=BLK).rearrange("p (t g) n -> p t g n", g=2)
        p_lo = hT_lo[:].rearrange("p k (a n) -> p (k a) n", n=BLK).rearrange("p (t g) n -> p t g n", g=2)
        const_loaded = sem("const_loaded_c")
        u_loaded = [sem(f"u_loaded{g}") for g in range(GROUPS)]
        m_filled, m_ready = sem("m_filled"), sem("m_ready")
        folded = sem("u_folded")
        p_filled, p_hi_done, p_lo_done = sem("p_filled"), sem("p_hi_done"), sem("p_lo_done")
        tab_loaded = [sem(f"tab_loaded{i}") for i in range(RT)]
        tab_used = sem("tab_used")
        y_filled, y_read = sem("f_filled"), sem("f_read")
        y_stored = [sem(f"f_stored{i}") for i in range(4)]
        wo_loaded = [sem(f"wo_loaded{i}") for i in range(2)]
        wo_hi_done, wo_lo_done = sem("wo_hi_done"), sem("wo_lo_done")
        out_blocks = [(b, first // 2 // P, n // 2 // P)
                      for first, n in SEQS[::-1] for b in range(first // BLK, (first + n) // BLK)]
        folded_tiles = [(first + l, first + n // 2 if l == 0 else None) for first, n in SEQS for l in range(0, n // 2, P)]
        FOLDS = 6 * len(SEQS)
        with nc.Block() as block:
            @block.sync
            def _(sp):
                sp.dma_start(wf[:], w_fnet).then_inc(const_loaded, 16)
                sp.dma_start(dft[:], channel_dft).then_inc(const_loaded, 16)
                for g in range(GROUPS):
                    sp.dma_start(uT[:, g], u_dram[g]).then_inc(u_loaded[g], 16)
                for k in range(KT):
                    if k >= 2:
                        sp.wait_ge(wo_lo_done, k - 1)
                    sp.dma_start(wo_raw[:, k % 2], w_out[k * P:(k + 1) * P]).then_inc(wo_loaded[k % 2], 16)
                for i, (b, _, _) in enumerate(out_blocks):
                    for g in range(GROUPS):
                        sp.wait_ge(y_read, GROUPS * i + g + 1)
                        sp.dma_start(y_dram[g, :, b * BLK:(b + 1) * BLK], out[:, g]).then_inc(y_stored[g], 16)
                for g in range(GROUPS):
                    sp.wait_ge(y_stored[g], 16 * NB)

            @block.gpsimd
            def _(pool):
                pool.wait_ge(u_loaded[GROUPS - 2], 16)
                for n in range(NTAB):
                    if n >= RT:
                        pool.wait_ge(tab_used, n - RT + 1)
                    pool.dma_start(tab[:, n % RT], tables[n]).then_inc(tab_loaded[n % RT], 16)

            @block.scalar
            def _(act):
                for g in range(GROUPS):
                    act.wait_ge(m_filled, g + 1)
                    nc.scalar.copy(m[:, g], banks[2 + g % 2][:, 0:2 * P]).then_inc(m_ready, 1)
                for f in range(2):
                    for t in range(HALF_TILES):
                        i = HALF_TILES * f + t
                        act.wait_ge(p_filled, i + 1)
                        nc.scalar.copy(p_hi[:, t, f], banks[4 + i % 4][:]).then_inc(p_hi_done, 1)
                act.wait_ge(p_filled, 2 * HALF_TILES)
                for k in range(KT):
                    act.wait_ge(wo_loaded[k % 2], 16 * (k // 2 + 1))
                    nc.scalar.copy(wo_hi[:, k], wo_raw[:, k % 2]).then_inc(wo_hi_done, 1)
                for i in range(NB):
                    for g in range(GROUPS):
                        act.wait_ge(y_filled, GROUPS * i + g + 1)
                        if i >= 1:
                            act.wait_ge(y_stored[g], 16 * i)
                        nc.scalar.copy(out[:, g], banks[4 * (i % 2) + g][:]).then_inc(y_read, 1)

            @block.vector
            def _(dve):
                for g in range(GROUPS):
                    dve.wait_ge(u_loaded[g], 16)
                    for first, n in SEQS:
                        e, u = even[:, g, first // 2:(first + n) // 2], uT[:, g, first:first + n]
                        nc.vector.tensor_copy(e[:, 0:1], u[:, 0:1]).then_inc(folded, 1)
                        nc.vector.tensor_tensor(e[:, 1:], u[:, 1:n // 2], u[:, n - 1:n // 2:-1], ALU.add)\
                            .then_inc(folded, 1)
                        nc.vector.tensor_tensor(u[:, 1:n // 2], u[:, 1:n // 2], u[:, n - 1:n // 2:-1], ALU.subtract)\
                            .then_inc(folded, 1)
                        dve.wait_ge(folded, FOLDS * g + (first > 0) * 6 + 3)
                        nc.vector.memset(u[:, 0:1], 0.0).then_inc(folded, 1)
                        nc.vector.memset(u[:, n // 2 + 1:n // 2 + P], 0.0).then_inc(folded, 2)
                for f in range(2):
                    for t in range(HALF_TILES):
                        i = HALF_TILES * f + t
                        dve.wait_ge(p_hi_done, i + 1)
                        nc.vector.tensor_tensor(p_lo[:, t, f], banks[4 + i % 4][:], p_hi[:, t, f].bitcast(F32),
                                                ALU.subtract).then_inc(p_lo_done, 1)
                for k in range(KT):
                    dve.wait_ge(wo_hi_done, k + 1)
                    nc.vector.tensor_tensor(wo_lo[:, k], wo_raw[:, k % 2], wo_hi[:, k].bitcast(F32),
                                            ALU.subtract).then_inc(wo_lo_done, 1)

            @block.tensor
            def _(pe):
                pe.wait_ge(const_loaded, 32)
                for g in range(GROUPS):
                    if g >= 2:
                        pe.wait_ge(m_ready, g - 1)
                    for w in range(2):
                        last = nc.tensor.matmul(banks[2 + g % 2][:, w * P:(w + 1) * P], dft[:, w], wf[:, g],
                                                start=(w == 0), stop=(w == 1), skip_group_check=True)
                    last.then_inc(m_filled, 1)
                pe.wait_ge(m_ready, GROUPS)
                for f in range(2):
                    for t, (first, middle) in enumerate(folded_tiles):
                        i = HALF_TILES * f + t
                        if i >= 4:
                            pe.wait_ge(p_lo_done, i - 3)
                        pe.wait_ge(folded, FOLDS * (2 * f + 2))
                        bank = banks[4 + i % 4]
                        for e in range(2):
                            g = 2 * f + e
                            cos, sin = bank[:, 2 * e * P:(2 * e + 1) * P], bank[:, (2 * e + 1) * P:(2 * e + 2) * P]
                            nc.tensor.matmul(cos, even[:, g, t * P:(t + 1) * P], m[:, g, 0], start=(e == 0), stop=False,
                                             skip_group_check=True)
                            last = nc.tensor.matmul(sin, uT[:, g, first:first + P], m[:, g, 1], start=False,
                                                    stop=(e == 1 and middle is None), skip_group_check=True)
                            if middle is not None:
                                last = nc.tensor.matmul(sin, uT[:, g, middle:middle + P], m[:, g, 0], start=False,
                                                        stop=(e == 1), skip_group_check=True)
                        last.then_inc(p_filled, 1)
                pe.wait_ge(p_lo_done, 2 * HALF_TILES)
                n = 0
                for i, (b, t0, nt) in enumerate(out_blocks):
                    if i >= 2:
                        pe.wait_ge(y_read, GROUPS * (i - 1))
                    for t in range(nt):
                        for w in range(2):
                            pe.wait_ge(tab_loaded[n % RT], 16 * (n // RT + 1))
                            for g in range(GROUPS):
                                at = slice(((g % 2) * 2 + w) * P, ((g % 2) * 2 + w + 1) * P)
                                ph, pl = p_hi[:, t0 + t, g // 2, at], p_lo[:, t0 + t, g // 2, at]
                                last = three_products(nc, banks[4 * (i % 2) + g][:], ph, pl, tab[:, n % RT, 0],
                                                      tab[:, n % RT, 1], t == 0 and w == 0, t == nt - 1 and w == 1)
                                if t == nt - 1 and w == 1 and g < GROUPS - 1:
                                    last.then_inc(y_filled, 1)
                            if t == nt - 1 and w == 1:
                                last.then_inc(y_filled, 1)
                                pe.wait_ge(y_filled, GROUPS * (i + 1))
                                pe.sem_inc(tab_used, 1)
                            else:
                                last.then_inc(tab_used, 1)
                            n += 1


def take_best(then, nc, table, best, where, rows, cols, slot):
    at, t = slice(8 * slot, 8 * slot + 8), table[rows, cols]
    then(nc.vector.max(best[rows, at], t))
    then(nc.vector.max_index(where[rows, at], best[rows, at], t))
    then(nc.vector.match_replace(t, best[rows, at], t, -2.0))


def output_phase(nc, x_dram, norm_ffn, w_router, identity, y_dram, acc, h_dram, routing, big_hi, big_lo, wo_hi, wo_lo):
    with ExitStack() as ctx:
        sb = lambda n, s, dt=F32: ctx.enter_context(nc.sbuf_tensor(n, s, dt))
        sem = lambda n: ctx.enter_context(nc.semaphore(n))
        pb = lambda n, s: ctx.enter_context(nc.psum_tensor(n, s, F32))
        table, best, where, token_of, gate_of = routing
        affinity = sb("affinity", [P, KT, ROWS])
        ORDER = list(range(CH, TT)) + list(range(CH))
        S_TILES = TT - CH
        RR = 4
        raw = sb("raw_d", [P, RR, BLK])
        x = sb("x_d", [P, 2, D])
        h = sb("h_d", [P, D])
        hT = sb("hT_d", [P, KT, P])
        nf = sb("nf", [P, D])
        wr = sb("wr", [P, KT, NE])
        ident = sb("ident_d", [P, P])
        stat = sb("stat_d", [P, 6, TT])
        ex = sb("ex_d", [P, NE])
        eps = sb("eps_d", [P, 1])
        ob = [pb(f"ob{i}", [P, BLK]) for i in range(4)]
        tb = [pb(f"tb{i}", [P, 4, P]) for i in range(2)]
        lg = pb("lg", [P, NE])
        rt = pb("rt", [ROWS, 4, P])
        SS, RMS, RSTD, NMAX, SUM, RSUM = range(6)
        pieces = [(k, t // CH) for t in ORDER[::CH] for k in range(KT)]
        const_loaded, set_up = sem("const_loaded_d"), sem("set_up_d")
        raw_loaded = [sem(f"raw_loaded_d{i}") for i in range(RR)]
        hi_done, lo_done = sem("hi_done_d"), sem("lo_done_d")
        x_loaded = [sem(f"x_loaded_d{i}") for i in range(2)]
        filled, added = sem("out_filled"), sem("x2_ready")
        x2_stored = [sem(f"x2_stored{i}") for i in range(2)]
        squared, rooted, inverted, h_ready, h_stored = (sem("x2_squared"), sem("x2_rooted"), sem("x2_inverted"),
                                                        sem("h2_ready"), sem("h2_stored"))
        transposed, hT_ready, routed = sem("h2_transposed"), sem("h2T_ready"), sem("logits_ready")
        negmax, exped, sum_inv, soft = sem("negmax"), sem("exped"), sem("sum_inv"), sem("affinity_ready")
        step = sem("dve_step_d")
        later_pieces = lambda t: range(min(KT + 3 * t, len(pieces)), min(KT + 3 * t + 3, len(pieces)))
        aff_turned, aff_copied = sem("aff_turned"), sem("aff_copied")
        xcols = lambda k, b: (slice(None), k, slice(b * BLK, (b + 1) * BLK))

        with nc.Block() as block:
            @block.sync
            def _(sp):
                for n, p in enumerate(pieces):
                    if n >= RR:
                        sp.wait_ge(lo_done, n - RR + 1)
                    k, b = p
                    sp.dma_start(raw[:, n % RR], y_dram[k, :, b * BLK:(b + 1) * BLK]).then_inc(raw_loaded[n % RR], 16)

            @block.gpsimd
            def _(pool):
                for buffer, value in ((affinity, -1.0), (table, -1.0), (best, 0.0), (gate_of, 0.0)):
                    nc.gpsimd.memset(buffer[:], value).then_inc(set_up, 1)
                for buffer in (where, token_of):
                    nc.gpsimd.memset(buffer[:].bitcast(F32), 0.0).then_inc(set_up, 1)
                nc.gpsimd.memset(eps[:], EPS).then_inc(set_up, 1)
                pool.dma_start(ident[:], identity).then_inc(const_loaded, 16)
                pool.dma_start(nf[:], norm_ffn.partition_broadcast(P)).then_inc(const_loaded, 16)
                pool.dma_start(wr[:], w_router.rearrange("(k p) e -> p k e", p=P)).then_inc(const_loaded, 16)
                for t in range(TT + 1):
                    if t < TT:
                        row = ORDER[t] * P
                        if t >= 2:
                            pool.wait_ge(x2_stored[t % 2], 16 * (t // 2))
                            pool.wait_ge(h_ready, t - 1)
                            pool.wait_ge(squared, t - 1)
                        pool.dma_start(x[:, t % 2], x_dram[row:row + P]).then_inc(x_loaded[t % 2], 16)
                    if t >= 1:
                        s = t - 1
                        row = ORDER[s] * P
                        pool.wait_ge(added, 2 * s + 2)
                        pool.dma_start(acc[row:row + P], x[:, s % 2]).then_inc(x2_stored[s % 2], 16)
                        pool.wait_ge(h_ready, s + 1)
                        pool.dma_start(h_dram[row:row + P], h[:]).then_inc(h_stored, 16)
                pool.wait_ge(h_stored, 16 * TT)
                for i in range(2):
                    pool.wait_ge(x2_stored[i], 16 * TT // 2)

            @block.scalar
            def _(act):
                def split(numbers):
                    for n in numbers:
                        act.wait_ge(raw_loaded[n % RR], 16 * (n // RR + 1))
                        nc.scalar.copy(big_hi[xcols(*pieces[n])], raw[:, n % RR]).then_inc(hi_done, 1)

                split(range(KT))
                act.wait_ge(set_up, 7)
                for t in range(TT):
                    split(later_pieces(t))
                    act.wait_ge(added, 2 * t + 2)
                    if t >= 1:
                        act.wait_ge(transposed, 2 * t)
                        act.wait_ge(routed, t)
                    nc.scalar.activation(hT[:].rearrange("p k t -> p (k t)"), x[:, t % 2], ACT.Square,
                                         accum_out=stat[:, SS, t:t + 1]).then_inc(squared, 1)
                    act.wait_ge(squared, t + 1)
                    nc.scalar.activation(stat[:, RMS, t:t + 1], stat[:, SS, t:t + 1], ACT.Sqrt, scale=1.0 / D,
                                         bias=eps[:]).then_inc(rooted, 1)
                    for f in range(2):
                        act.wait_ge(transposed, 2 * t + f + 1)
                        nc.scalar.copy(hT[:, 4 * f:4 * f + 4], tb[f][:]).then_inc(hT_ready, 1)
                    act.wait_ge(negmax, t + 1)
                    if t >= 1:
                        act.wait_ge(soft, t)
                    nc.scalar.activation(ex[:], lg[:], ACT.Exp, bias=stat[:, NMAX, t:t + 1],
                                         accum_out=stat[:, SUM, t:t + 1]).then_inc(exped, 1)

            @block.vector
            def _(dve):
                own = 0

                def then(ins):
                    nonlocal own
                    own += 1
                    ins.then_inc(step, 1)
                    dve.wait_ge(step, own)

                def sample_rounds(pause):
                    for i in range(sum(EARLY_ROUNDS[:pause]), sum(EARLY_ROUNDS[:pause + 1])):
                        take_best(then, nc, table, best, where, slice(0, NE), slice(0, SEQS[1][1]), i)

                def split(numbers):
                    for n in numbers:
                        at = xcols(*pieces[n])
                        dve.wait_ge(hi_done, n + 1)
                        nc.vector.tensor_tensor(big_lo[at], raw[:, n % RR], big_hi[at].bitcast(F32), ALU.subtract)\
                            .then_inc(lo_done, 1)

                split(range(KT))
                dve.wait_ge(set_up, 7)
                dve.wait_ge(const_loaded, 48)
                for t in range(TT):
                    split(later_pieces(t))
                    dve.wait_ge(x_loaded[t % 2], 16 * (t // 2 + 1))
                    for f in range(2):
                        dve.wait_ge(filled, 2 * t + f + 1)
                        cols = slice(f * BLK, (f + 1) * BLK)
                        nc.vector.tensor_tensor(x[:, t % 2, cols], x[:, t % 2, cols], ob[(2 * t + f) % 4][:], ALU.add)\
                            .then_inc(added, 1)
                    if t > S_TILES:
                        sample_rounds(3 * (t - S_TILES) - 2)
                    dve.wait_ge(rooted, t + 1)
                    nc.vector.reciprocal(stat[:, RSTD, t:t + 1], stat[:, RMS, t:t + 1]).then_inc(inverted, 1)
                    dve.wait_ge(inverted, t + 1)
                    dve.wait_ge(added, 2 * t + 2)
                    if t >= 1:
                        dve.wait_ge(transposed, 2 * t)
                        dve.wait_ge(h_stored, 16 * t)
                    nc.vector.scalar_tensor_tensor(out=h[:], in0=x[:, t % 2], scalar=stat[:, RSTD, t:t + 1], in1=nf[:],
                                                   op0=ALU.mult, op1=ALU.mult).then_inc(h_ready, 1)
                    if t > S_TILES:
                        sample_rounds(3 * (t - S_TILES) - 1)
                    dve.wait_ge(routed, t + 1)
                    then(nc.vector.reduce_max(stat[:, RSUM, t:t + 1], lg[:], AX_X))
                    nc.vector.tensor_scalar(stat[:, NMAX, t:t + 1], stat[:, RSUM, t:t + 1], -1.0, None, ALU.mult)\
                        .then_inc(negmax, 1)
                    dve.wait_ge(exped, t + 1)
                    nc.vector.reciprocal(stat[:, RSUM, t:t + 1], stat[:, SUM, t:t + 1]).then_inc(sum_inv, 1)
                    dve.wait_ge(sum_inv, t + 1)
                    at = affinity[:, t, 0:NE] if t < S_TILES else affinity[:, t - S_TILES, PROMPT_ROW:ROWS]
                    nc.vector.tensor_scalar(at, ex[:], stat[:, RSUM, t:t + 1], None, ALU.mult).then_inc(soft, 1)
                    if t == S_TILES:
                        for i in range(2):
                            dve.wait_ge(aff_turned, i + 1)
                            nc.vector.tensor_copy(table[0:NE, i * BLK:(i + 1) * BLK], rt[0:NE].rearrange("e k t -> e (k t)"))\
                                .then_inc(aff_copied, 1)
                        dve.wait_ge(aff_copied, 2)
                    if t >= S_TILES and t + 1 < TT:
                        sample_rounds(3 * (t - S_TILES))
                dve.wait_ge(aff_turned, 3)
                nc.vector.tensor_copy(table[PROMPT_ROW:ROWS, 0:BLK], rt[PROMPT_ROW:ROWS].rearrange("e k t -> e (k t)"))\
                    .then_inc(aff_copied, 1)
                dve.wait_ge(aff_copied, 3)

            @block.tensor
            def _(pe):
                def product(t):
                    b = t // CH
                    row = ORDER[t] * P
                    for f in range(2):
                        n = 2 * t + f
                        if n >= 4:
                            pe.wait_ge(added, n - 3)
                        for k in range(KT):
                            if t % CH == 0 and f == 0:
                                pe.wait_ge(lo_done, b * KT + k + 1)
                            cols = slice(row, row + P)
                            half = slice(f * BLK, (f + 1) * BLK)
                            last = three_products(nc, ob[n % 4][:], big_hi[:, k, cols], big_lo[:, k, cols],
                                                  wo_hi[:, k, half], wo_lo[:, k, half], k == 0, k == KT - 1)
                        last.then_inc(filled, 1)

                def turn_affinities(count, rows, first):
                    pe.wait_ge(soft, count)
                    for i in range(4):
                        last = nc.tensor.transpose(rt[rows, i], affinity[:, first + i, rows], ident[:])
                    last.then_inc(aff_turned, 1)

                product(0)
                pe.wait_ge(const_loaded, 48)
                for t in range(TT):
                    if t + 1 < TT:
                        product(t + 1)
                    pe.wait_ge(h_ready, t + 1)
                    for f in range(2):
                        if t >= 1:
                            pe.wait_ge(hT_ready, 2 * (t - 1) + f + 1)
                        for k in range(4):
                            last = nc.tensor.transpose(tb[f][:, k], h[:, (4 * f + k) * P:(4 * f + k + 1) * P], ident[:])
                        last.then_inc(transposed, 1)
                    pe.wait_ge(hT_ready, 2 * t + 2)
                    if t >= 1:
                        pe.wait_ge(exped, t)
                    for k in range(KT):
                        last = nc.tensor.matmul(lg[:], hT[:, k], wr[:, k], start=(k == 0), stop=(k == KT - 1))
                    last.then_inc(routed, 1)
                    if t == S_TILES:
                        turn_affinities(S_TILES, slice(0, NE), 0)
                        pe.wait_ge(aff_copied, 1)
                        turn_affinities(S_TILES, slice(0, NE), 4)
                pe.wait_ge(aff_copied, 2)
                turn_affinities(TT, slice(0, ROWS), 0)


def experts_phase(nc, weights, identity, h_dram, acc, routing, big_hi, big_lo):
    with ExitStack() as ctx:
        sb = lambda n, s, dt=F32: ctx.enter_context(nc.sbuf_tensor(n, s, dt))
        sem = lambda n: ctx.enter_context(nc.semaphore(n))
        pb = lambda n, s: ctx.enter_context(nc.psum_tensor(n, s, F32))
        RAW, RING, TB = 3, 3, 4
        FT = FF // P
        FB = FF // BLK
        GROUPS_E = 2 * FB + 2
        TURNS = 2 * FB + KT // 2
        FIRST = KT // 2
        raw = sb("ew_raw", [P, RAW, KT, BLK])
        table, best, where, token_of, gate_of = routing
        w_hi, w_lo = (big[:].rearrange("p k t -> p (k t)").rearrange("p (r k n) -> p r k n", r=RING, k=KT)
                      for big in (big_hi, big_lo))
        xs, xp = sb("xs", [CAP_S, D]), sb("xp", [CAP_P, D])
        x = sb("x_parts", [P, KT, 2 * CAP], F32R)
        h = sb("h_parts", [P, FT, 2 * CAP], F32R)
        silu_s, silu_p = sb("silu_s", [CAP_S, BLK]), sb("silu_p", [CAP_P, BLK])
        low = sb("low", [CAP_P, BLK])
        hs, hp = sb("hs", [CAP_S, BLK]), sb("hp", [CAP_P, BLK])
        where_f = hs[0:ROWS, 0:CAP_S]
        ys, yp = table, sb("yp", [CAP_P, D])
        next_token, this_token = sb("next_token", [P, 2], U32), sb("this_token", [P, 2], U32)
        this_gate = sb("this_gate", [P, 2])
        ident = sb("ident_f", [P, P])
        s_bank = [pb(f"s_bank{i}", [P, BLK]) for i in range(2)]
        p_bank = [pb(f"p_bank{i}", [P, BLK]) for i in range(2)]
        tb = [pb(f"etb{i}", [P, 2, CAP]) for i in range(TB)]
        const_loaded = sem("const_loaded_f")
        raw_loaded = [sem(f"ew_loaded{i}") for i in range(RAW)]
        hi_done = sem("ew_hi_done")
        lo_done = sem("ew_lo_done")
        chunk_done = sem("chunk_done")
        low_done = sem("low_done")
        silu_ready = sem("silu_ready")
        taken = sem("taken")
        step = sem("dve_step_f")
        turned = sem("turned")
        turned_hi = sem("turned_hi")
        turned_lo = sem("turned_lo")
        picked, gathered = sem("tokens_picked"), sem("x_gathered")
        ys_ready, yp_ready, scattered = sem("ys_ready"), sem("yp_ready"), sem("y_scattered")
        rows_free = sem("rows_free")
        choosing, chosen, back = sem("choosing"), sem("chosen"), sem("turned_back")
        tokens_ready = sem("tokens_ready")
        pool_passed = sem("pool_passed")
        EARLY = sum(EARLY_ROUNDS)
        S_SLOTS, P_SLOTS = CAP_S // 8, CAP_P // 8
        S_HI, P_BOTH, S_LO = slice(0, P), slice(P, 2 * P), slice(2 * P, 3 * P)

        def experts(eng, body):
            with eng.Fori(0, NE - 1) as e:
                body(e, True)
            body(NE - 1, False)

        with nc.Block() as block:
            @block.sync
            def _(sp):
                sp.dma_start(ident[:], identity).then_inc(const_loaded, 16)
                with sp.Fori(0, NE) as e:
                    for c in range(CHUNKS):
                        sp.wait_ge(lo_done, e * CHUNKS + c + 1)
                        sp.dma_start(raw[:, c % RAW], weights[e, c]).then_inc(raw_loaded[c % RAW], 16)

            @block.gpsimd
            def _(pool):
                def rows():
                    pool.indirect_dma_start(xs[:], None, h_dram, bass.IndirectOffsetOnAxis(next_token[:, 0:1], 0))\
                        .then_inc(gathered, 16)
                    pool.indirect_dma_start(xp[:], None, h_dram, bass.IndirectOffsetOnAxis(next_token[0:CAP_P, 1:2], 0))\
                        .then_inc(gathered, 16)

                pool.sem_inc(rows_free, 1)
                pool.wait_ge(hi_done, 1)
                nc.gpsimd.tensor_tensor(w_lo[:, 0], raw[:, 0], w_hi[:, 0].bitcast(F32), ALU.subtract).then_inc(lo_done, 1)
                pool.wait_ge(tokens_ready, 4)
                nc.gpsimd.tensor_copy(next_token[:], token_of[:, 0, :]).then_inc(picked, 1)
                pool.wait_ge(picked, 1)
                rows()

                def body(e, more):
                    pool.wait_ge(gathered, e * 32 + 32)
                    pool.sem_inc(pool_passed, 1)
                    nc.gpsimd.tensor_copy(this_token[:], next_token[:]).then_inc(picked, 1)
                    nc.gpsimd.tensor_copy(this_gate[:].unsqueeze(1), gate_of[:, bass.ds(e, 1), :]).then_inc(picked, 1)
                    if more:
                        pool.wait_ge(picked, e * 3 + 3)
                        pool.wait_ge(turned, e * TURNS + FIRST)
                        pool.sem_inc(pool_passed, 1)
                        nc.gpsimd.tensor_copy(next_token[:].unsqueeze(1), token_of[:, bass.ds(e + 1, 1), :]).then_inc(picked, 1)
                        pool.wait_ge(picked, e * 3 + 4)
                        pool.sem_inc(pool_passed, 1)
                        rows()
                    pool.wait_ge(ys_ready, e * 2 + 2)
                    pool.wait_ge(yp_ready, e * 2 + 2)
                    pool.sem_inc(pool_passed, 1)
                    pool.indirect_dma_start(acc, bass.IndirectOffsetOnAxis(this_token[:, 0:1], 0), ys[:], None,
                                            compute_op=ALU.add).then_inc(scattered, 16)
                    pool.indirect_dma_start(acc, bass.IndirectOffsetOnAxis(this_token[0:CAP_P, 1:2], 0), yp[:], None,
                                            compute_op=ALU.add).then_inc(scattered, 16)
                    pool.wait_ge(scattered, e * 32 + 32)
                    pool.sem_inc(rows_free, 1)

                experts(pool, body)

            @block.scalar
            def _(act):
                def split(e, c):
                    act.wait_ge(raw_loaded[c % RAW], (e * (CHUNKS // RAW) + c // RAW + 1) * 16)
                    act.wait_ge(chunk_done, e * CHUNKS + c + 1)
                    nc.scalar.copy(w_hi[:, c % RING], raw[:, c % RAW]).then_inc(hi_done, 1)

                def high(dst, first, use):
                    act.wait_ge(turned, use + 1)
                    nc.scalar.copy(dst[:, first:first + 2, 0:CAP], tb[first // 2 % TB][:]).then_inc(turned_hi, 1)

                def low_half(e, g):
                    act.wait_ge(taken, e * GROUPS_E + g + 2)
                    nc.scalar.copy(low[:], p_bank[g % 2][CAP_P:2 * CAP_P]).then_inc(low_done, 1)

                for c in range(2):
                    split(0, c)
                for r in range(KT // 2):
                    high(x, 2 * r, r)

                def body(e, more):
                    for c in range(CHUNKS):
                        if c + 2 < CHUNKS:
                            split(e, c + 2)
                        elif more:
                            split(e + 1, c + 2 - CHUNKS)
                        act.wait_ge(chunk_done, e * CHUNKS + c + 1 + RING)
                        if c < 2 * FB and c % 2 == 0:
                            act.wait_ge(taken, e * GROUPS_E + c + 2)
                            nc.scalar.activation(silu_s[:], s_bank[0][:], ACT.Silu).then_inc(silu_ready, 1)
                            low_half(e, c)
                            act.wait_ge(taken, e * GROUPS_E + c + 3)
                            nc.scalar.activation(silu_p[:], silu_p[:], ACT.Silu).then_inc(silu_ready, 1)
                            if c >= 2:
                                for r in range(2):
                                    t = 2 * (c // 2 - 1) + r
                                    high(h, 2 * t, e * TURNS + FIRST + t)
                        elif c < 2 * FB:
                            low_half(e, c)
                        elif c == 2 * FB:
                            for r in range(2):
                                t = 2 * (FB - 1) + r
                                high(h, 2 * t, e * TURNS + FIRST + t)
                        elif c % 2 == 1:
                            i = (c - 2 * FB) // 2
                            act.wait_ge(picked, e * 3 + 3)
                            act.wait_ge(rows_free, e + 1)
                            nc.scalar.activation(ys[:, i * BLK:(i + 1) * BLK], s_bank[i][:], ACT.Identity,
                                                 scale=this_gate[:, 0:1]).then_inc(ys_ready, 1)
                            low_half(e, 2 * FB + i)
                            if i == 0 and more:
                                for r in range(KT // 2):
                                    high(x, 2 * r, e * TURNS + FIRST + 2 * FB + r)

                experts(act, body)

            @block.vector
            def _(dve):
                dve.sem_inc(lo_done, RAW)
                dve.sem_inc(taken, 2)
                dve.sem_inc(turned_lo, TB)

                def split(e, c):
                    dve.wait_ge(hi_done, e * CHUNKS + c + 1)
                    nc.vector.tensor_tensor(w_lo[:, c % RING], raw[:, c % RAW], w_hi[:, c % RING].bitcast(F32),
                                            ALU.subtract).then_inc(lo_done, 1)

                def lows(dst, first, use):
                    dve.wait_ge(turned_hi, use + 1)
                    bank, tiles = tb[first // 2 % TB], slice(first, first + 2)
                    nc.vector.tensor_tensor(dst[:, tiles, S_LO], bank[:, :, 0:CAP_S], dst[:, tiles, S_HI].bitcast(F32),
                                            ALU.subtract)
                    nc.vector.tensor_tensor(dst[:, tiles, CAP:CAP + CAP_P], bank[:, :, CAP_S:CAP],
                                            dst[:, tiles, CAP_S:CAP].bitcast(F32), ALU.subtract).then_inc(turned_lo, 1)

                chosen_steps = 0

                def choose(ins):
                    nonlocal chosen_steps
                    chosen_steps += 1
                    ins.then_inc(choosing, 1)
                    dve.wait_ge(choosing, chosen_steps)

                for i in range(EARLY, S_SLOTS):
                    take_best(choose, nc, table, best, where, slice(0, ROWS), slice(0, SEQS[1][1]), i)
                for i in range(S_SLOTS - P_SLOTS, EARLY):
                    take_best(choose, nc, table, best, where, slice(PROMPT_ROW, ROWS), slice(0, SEQS[0][1]), i)
                nc.vector.tensor_copy(where_f, where[:]).then_inc(chosen, 1)
                dve.wait_ge(back, 4)
                nc.vector.tensor_scalar(token_of[:, 0:NE, 0], s_bank[0][:, ROWS:ROWS + NE], float(SEQS[1][0]), None,
                                        ALU.add).then_inc(tokens_ready, 1)
                nc.vector.tensor_copy(token_of[0:CAP_P, 0:NE, 1], p_bank[0][0:CAP_P, ROWS + PROMPT_ROW:2 * ROWS])\
                    .then_inc(tokens_ready, 1)
                nc.vector.tensor_copy(gate_of[:, :, 0], s_bank[0][:, 0:NE]).then_inc(tokens_ready, 1)
                nc.vector.tensor_copy(gate_of[0:CAP_P, :, 1], p_bank[0][0:CAP_P, PROMPT_ROW:ROWS]).then_inc(tokens_ready, 1)
                for r in range(KT // 2):
                    lows(x, 2 * r, r)
                dve.wait_ge(lo_done, RAW + 1)
                split(0, 1)

                def body(e, more):
                    steps = 0

                    def then(ins):
                        nonlocal steps
                        steps += 1
                        ins.then_inc(step, 1)
                        dve.wait_ge(step, e * (2 * FB + 2) + steps)

                    for c in range(CHUNKS):
                        if c + 2 < CHUNKS:
                            split(e, c + 2)
                        elif more:
                            split(e + 1, c + 2 - CHUNKS)
                        if c < 2 * FB:
                            dve.wait_ge(low_done, e * GROUPS_E + c + 1)
                            if c % 2 == 0:
                                nc.vector.tensor_tensor(silu_p[:], p_bank[0][0:CAP_P], low[:], ALU.add).then_inc(taken, 1)
                                if c >= 2:
                                    for r in range(2):
                                        t = 2 * (c // 2 - 1) + r
                                        lows(h, 2 * t, e * TURNS + FIRST + t)
                            else:
                                b = c // 2
                                dve.wait_ge(turned, e * TURNS + FIRST + 2 * b)
                                dve.wait_ge(silu_ready, e * 2 * FB + 2 * b + 2)
                                then(nc.vector.tensor_tensor(hp[:], p_bank[1][0:CAP_P], low[:], ALU.add))
                                then(nc.vector.tensor_tensor(hp[:], hp[:], silu_p[:], ALU.mult))
                                nc.vector.tensor_tensor(hs[:], silu_s[:], s_bank[1][:], ALU.mult).then_inc(taken, 1)
                        elif c == 2 * FB:
                            for r in range(2):
                                t = 2 * (FB - 1) + r
                                lows(h, 2 * t, e * TURNS + FIRST + t)
                        elif c % 2 == 1:
                            i = (c - 2 * FB) // 2
                            dve.wait_ge(low_done, e * GROUPS_E + 2 * FB + i + 1)
                            y = yp[:, i * BLK:(i + 1) * BLK]
                            then(nc.vector.tensor_tensor(y, p_bank[i][0:CAP_P], low[:], ALU.add))
                            dve.sem_inc(taken, 1)
                            nc.vector.tensor_scalar(y, y, this_gate[0:CAP_P, 1:2], None, ALU.mult).then_inc(yp_ready, 1)
                            if i == 0 and more:
                                for r in range(KT // 2):
                                    lows(x, 2 * r, e * TURNS + FIRST + 2 * FB + r)

                experts(dve, body)

            @block.tensor
            def _(pe):
                def turn(bank, src_s, src_p, first, use):
                    pe.wait_ge(turned_lo, use + 1)
                    for i in range(2):
                        cols = slice((first + i) * P, (first + i + 1) * P)
                        nc.tensor.transpose(bank[:, i, 0:CAP_S], src_s[:, cols], ident[:])
                        last = nc.tensor.transpose(bank[:, i, CAP_S:CAP], src_p[:, cols], ident[0:CAP_P, 0:CAP_P])
                    last.then_inc(turned, 1)

                def turn_x(e, use):
                    pe.wait_ge(gathered, e * 32 + 32)
                    for r in range(KT // 2):
                        turn(tb[r % TB], xs, xp, 2 * r, use + r)

                def turn_h(e, b):
                    pe.wait_ge(taken, e * GROUPS_E + 2 * b + 4)
                    for r in range(2):
                        t = 2 * b + r
                        turn(tb[t % TB], hs, hp, 2 * r, e * TURNS + FIRST + t)

                def chunk(c, operand, tiles, i, start, stop, pause=None):
                    for k, t in enumerate(tiles):
                        if pause and k == KT // 2:
                            pause()
                        hi, lo = w_hi[:, c % RING, k], w_lo[:, c % RING, k]
                        a, b = start and k == 0, stop and k == KT - 1
                        nc.tensor.matmul(s_bank[i][:], operand[:, t, S_HI], hi, start=a, stop=False)
                        nc.tensor.matmul(s_bank[i][:], operand[:, t, S_LO], hi, start=False, stop=False)
                        nc.tensor.matmul(s_bank[i][:], operand[:, t, S_HI], lo, start=False, stop=b)
                        nc.tensor.matmul(p_bank[i][:], operand[:, t, P_BOTH], hi, start=a, stop=False)
                        last = nc.tensor.matmul(p_bank[i][:], operand[:, t, P_BOTH], lo, start=False, stop=b)
                    last.then_inc(chunk_done, 1)

                pe.sem_inc(chunk_done, RING)
                pe.wait_ge(const_loaded, 16)
                pe.wait_ge(chosen, 1)
                for i, rows in enumerate((best, where_f)):
                    nc.tensor.transpose(s_bank[0][:, i * ROWS:(i + 1) * ROWS], rows[:, 0:CAP_S], ident[0:ROWS, 0:ROWS])\
                        .then_inc(back, 1)
                    nc.tensor.transpose(p_bank[0][0:CAP_P, i * ROWS:(i + 1) * ROWS], rows[:, CAP_S - CAP_P:CAP_S],
                                        ident[0:ROWS, 0:ROWS]).then_inc(back, 1)
                turn_x(0, 0)

                def body(e, more):
                    pe.wait_ge(turned_lo, e * TURNS + FIRST + TB)
                    for c in range(2 * FB):
                        pe.wait_ge(lo_done, e * CHUNKS + c + 1 + RAW)
                        pe.wait_ge(taken, e * GROUPS_E + c + 1)
                        chunk(c, x, range(KT), c % 2, True, True)
                        if c >= 2 and c % 2 == 0:
                            turn_h(e, c // 2 - 1)
                    for c in range(2 * FB, CHUNKS):
                        half, part = (c - 2 * FB) // 2, c % 2
                        pe.wait_ge(lo_done, e * CHUNKS + c + 1 + RAW)
                        if part == 0:
                            pe.wait_ge(taken, e * GROUPS_E + 2 * FB + half + 1)
                        ready = e * TURNS + FIRST + TB + 2 * FB
                        pe.wait_ge(turned_lo, ready - (4 if c == 2 * FB else 2 if c == 2 * FB + 1 else 0))
                        pause = (lambda: pe.wait_ge(turned_lo, ready)) if c == 2 * FB + 1 else None
                        chunk(c, h, range(part * KT, (part + 1) * KT), half, part == 0, part == 1, pause)
                        if c == 2 * FB:
                            turn_h(e, FB - 1)
                        if c == 2 * FB + 1 and more:
                            turn_x(e + 1, e * TURNS + FIRST + 2 * FB)

                experts(pe, body)


def final_phase(nc, acc, norm_final, outs):
    with ExitStack() as ctx:
        sb = lambda n, s, dt=F32: ctx.enter_context(nc.sbuf_tensor(n, s, dt))
        sem = lambda n: ctx.enter_context(nc.semaphore(n))
        R = 4
        x = sb("x_g", [P, R, D])
        sq = sb("sq_g", [P, 2, D])
        y = sb("y_g", [P, R, D])
        nw = sb("nw_g", [P, D])
        ss, rms, rstd, eps = sb("ss_g", [P, TT]), sb("rms_g", [P, TT]), sb("rstd_g", [P, TT]), sb("eps_g", [P, 1])
        const_loaded, eps_set = sem("const_loaded_g"), sem("eps_set_g")
        loaded = [sem(f"loaded_g{i}") for i in range(R)]
        stored = [sem(f"stored_g{i}") for i in range(R)]
        squared, rooted, inverted, ready = sem("squared_g"), sem("rooted_g"), sem("inverted_g"), sem("ready_g")
        with nc.Block() as block:
            @block.sync
            def _(sp):
                sp.dma_start(nw[:], norm_final.partition_broadcast(P)).then_inc(const_loaded, 16)
                for t in range(TT):
                    if t >= R:
                        sp.wait_ge(ready, t - R + 1)
                    sp.dma_start(x[:, t % R], acc[t * P:(t + 1) * P]).then_inc(loaded[t % R], 16)

            @block.gpsimd
            def _(pool):
                for t in range(TT):
                    pool.wait_ge(ready, t + 1)
                    out, row = (outs[0], t) if t < CH else (outs[1], t - CH)
                    pool.dma_start(out[row * P:(row + 1) * P], y[:, t % R]).then_inc(stored[t % R], 16)
                for i in range(R):
                    pool.wait_ge(stored[i], 16 * TT // R)

            @block.scalar
            def _(act):
                act.wait_ge(eps_set, 1)
                for t in range(TT):
                    act.wait_ge(loaded[t % R], 16 * (t // R + 1))
                    if t >= 2:
                        act.wait_ge(squared, t - 1)
                    nc.scalar.activation(sq[:, t % 2], x[:, t % R], ACT.Square, accum_out=ss[:, t:t + 1]).then_inc(squared, 1)
                    act.wait_ge(squared, t + 1)
                    nc.scalar.activation(rms[:, t:t + 1], ss[:, t:t + 1], ACT.Sqrt, scale=1.0 / D,
                                         bias=eps[:]).then_inc(rooted, 1)

            @block.vector
            def _(dve):
                nc.vector.memset(eps[:], EPS).then_inc(eps_set, 1)
                dve.wait_ge(const_loaded, 16)
                for t in range(TT):
                    dve.wait_ge(rooted, t + 1)
                    nc.vector.reciprocal(rstd[:, t:t + 1], rms[:, t:t + 1]).then_inc(inverted, 1)
                    dve.wait_ge(inverted, t + 1)
                    if t >= R:
                        dve.wait_ge(stored[t % R], 16 * (t // R))
                    nc.vector.scalar_tensor_tensor(out=y[:, t % R], in0=x[:, t % R], scalar=rstd[:, t:t + 1], in1=nw[:],
                                                   op0=ALU.mult, op1=ALU.mult).then_inc(ready, 1)


def encoder(nc, x, norm_mix, w_heads, w_fnet, lb_params, out_norm, w_out, norm_ffn, w_router, expert_weights,
            norm_final, identity, masks, channel_dft, tables, out_prompt, out_sample):
    y_dram = nc.dram_tensor("mixer_y", (KT, P, NT), F32, kind="Internal").ap()
    u_dram = nc.dram_tensor("fnet_u", (GROUPS, P, NT), F32, kind="Internal").ap()
    acc = nc.dram_tensor("residual", (NT, D), F32, kind="Internal").ap()
    h_dram = nc.dram_tensor("ffn_in", (NT, D), F32, kind="Internal").ap()
    with ExitStack() as ctx:
        sb = lambda n, s, dt=F32: ctx.enter_context(nc.sbuf_tensor(n, s, dt))
        big_hi = sb("big_hi", [P, KT, NT], F32R)
        big_lo = sb("big_lo", [P, KT, NT], F32R)
        with ExitStack() as held:
            weights = HeadWeights(nc, lambda n, s, dt=F32: held.enter_context(nc.sbuf_tensor(n, s, dt)),
                                  lambda n: held.enter_context(nc.semaphore(n)), w_heads)
            input_norm_phase(nc, x, norm_mix, identity, weights, big_hi, big_lo)
            heads_phase(nc, weights, lb_params, out_norm, identity, masks, big_hi, big_lo, y_dram[GROUPS:], u_dram)
        routing = (sb("table", [P, D]), sb("best", [ROWS, CAP_S]), sb("where", [ROWS, CAP_S], U32),
                   sb("token_of", [P, NE, 2], U32), sb("gate_of", [P, NE, 2]))
        with nc.sbuf_tensor("u_space", [P, 2 * KT, D], F32) as u_space:
            pass
        with nc.sbuf_tensor("wo_hi", [P, KT, D], F32R) as wo_hi, nc.sbuf_tensor("wo_lo", [P, KT, D], F32R) as wo_lo:
            fourier_phase(nc, u_dram, w_fnet, channel_dft, tables, w_out, big_hi, big_lo, u_space, wo_hi,
                          wo_lo, y_dram)
            output_phase(nc, x, norm_ffn, w_router, identity, y_dram, acc, h_dram, routing, big_hi, big_lo, wo_hi, wo_lo)
        experts_phase(nc, expert_weights, identity, h_dram, acc, routing, big_hi, big_lo)
        final_phase(nc, acc, norm_final, (out_prompt, out_sample))


def constants():
    s = np.arange(P)
    masks = np.stack([((s[:, None] >> (l + 1)) == (s >> (l + 1))) & ((s[:, None] >> l) != (s >> l))
                      for l in range(LEVELS)], 1).astype(np.float32)
    angle = 2 * np.pi * np.outer(s, s) / P
    channel_dft = (np.stack([np.cos(angle), np.sin(angle)], 1) / np.sqrt(P)).astype(np.float32)
    tables = []
    for _, n in SEQS[::-1]:
        for k0 in range(0, n, BLK):
            for l0 in range(0, n // 2, P):
                turn = np.outer(np.arange(l0, l0 + P), np.arange(k0, k0 + BLK)) % n
                angle = 2 * np.pi * turn / n
                minus_sine = -np.sin(angle)
                if l0 == 0:
                    minus_sine[0] = np.cos(np.pi * np.arange(k0, k0 + BLK))
                for part in (np.cos(angle), minus_sine):
                    full = (part / np.sqrt(n)).astype(np.float32)
                    bits = full.view(np.uint32)
                    high = ((bits + 0x800) & np.uint32(0xFFFFF000)).view(np.float32)
                    tables.append(np.stack([high, full - high], 1))
    return np.eye(P, dtype=np.float32), masks, channel_dft, np.stack(tables)


def kernel(**inputs):
    import concourse.bacc as bacc
    from concourse.bass_utils import run_bass_kernel_spmd

    a = {k: np.asarray(v) for k, v in inputs.items()}
    identity, masks, channel_dft, tables = constants()
    weights = np.empty((NE, CHUNKS, P, KT, BLK), np.float32)
    for i, name in enumerate(("w_gate", "w_up")):
        weights[:, i:8:2] = a[name][0].reshape(NE, KT, P, FF // BLK, BLK).transpose(0, 3, 2, 1, 4)
    weights[:, 8:] = a["w_down"][0].reshape(NE, 2, KT, P, D // BLK, BLK).transpose(0, 4, 1, 3, 2, 5)\
        .reshape(NE, 4, P, KT, BLK)
    arrays = {
        "x": np.concatenate([a["x_prompt"][0], a["x_sample"][0]]),
        "norm_mix": a["norm_mix"][0],
        "w_heads": np.ascontiguousarray(a["w_in"][0].reshape(KT, P, 6, HEADS, P).transpose(3, 1, 2, 0, 4)),
        "w_fnet": np.ascontiguousarray(a["w_fnet"][0].transpose(1, 0, 2)),
        "lb_params": np.ascontiguousarray(
            np.stack([a["lb_fwd"][0].reshape(HEADS, P), a["lb_bwd"][0].reshape(HEADS, P)]).transpose(2, 0, 1)),
        "out_norm": a["hgrn_out_norm"].reshape(P, 1),
        "w_out": a["w_out"][0],
        "norm_ffn": a["norm_ffn"][0],
        "w_router": a["w_router"][0],
        "expert_weights": weights,
        "norm_final": a["norm_final"],
        "identity": identity, "masks": masks, "channel_dft": channel_dft, "tables": tables,
    }
    nc = bacc.Bacc("TRN2", target_bir_lowering=False, num_devices=1)
    args = [nc.dram_tensor(f"in_{n}", v.shape, mybir.dt.from_np(v.dtype), kind="ExternalInput").ap()
            for n, v in arrays.items()]
    args += [nc.dram_tensor(f"out_{n}", (length, D), F32, kind="ExternalOutput").ap()
             for n, (_, length) in zip(("prompt", "sample"), SEQS)]
    encoder(nc, *args)
    r = run_bass_kernel_spmd(nc, [{f"in_{n}": v for n, v in arrays.items()}], core_ids=[0])
    return r.results[0]["out_prompt"][None], r.results[0]["out_sample"][None]
```
